# Optimizing a Trainium2 kernel written in Bass

```python
import jax, jax.numpy as jnp
from jax import lax
import numpy as np

D_MODEL = 1024
BATCH = 1
SEQ = 128
DEPTH = 1
DEC_BATCH = 1
DEC_SEQ = 512
PAST_LEN = 128

GRID_W = 64
D_RNN = 1024
RNN_HEADS = 16
RNN_HB = D_RNN // RNN_HEADS
CONV_W = 4
RG_C = 8.0
D_POOL = 512
POOL_WINDOWS = (2, 4, 8, 16)
POOL_GROUPS = 4
POOL_GW = D_POOL // POOL_GROUPS
D_IN = 2 * D_RNN + D_POOL + 2 * D_MODEL
PEER_HEADS = 8
PEER_DKEY = 256
PEER_DHALF = PEER_DKEY // 2
N_KEYS = 128
N_EXPERTS = N_KEYS * N_KEYS
PEER_TOPK = 16
PEER_BLOCK = 128
EPS = 1e-6
POS_BASE = 10000.0

kernel_name = 'hybrid_rglru_pool_peer_flow_step'

def rmsnorm(x, g):
    xf = x.astype(jnp.float32)
    y = xf * lax.rsqrt(jnp.mean(xf * xf, axis=-1, keepdims=True) + EPS)
    return (y * g.astype(jnp.float32)).astype(x.dtype)

def grid_pos_embed(n_tokens, dtype):
    rows = n_tokens // GRID_W
    nq = D_MODEL // 4
    omega = 1.0 / (POS_BASE ** (jnp.arange(nq, dtype=jnp.float32) / nq))
    r = jnp.broadcast_to(jnp.arange(rows, dtype=jnp.float32)[:, None], (rows, GRID_W)).reshape(-1)
    col = jnp.broadcast_to(jnp.arange(GRID_W, dtype=jnp.float32)[None, :], (rows, GRID_W)).reshape(-1)
    er = r[:, None] * omega[None, :]
    ec = col[:, None] * omega[None, :]
    return jnp.concatenate([jnp.sin(er), jnp.cos(er), jnp.sin(ec), jnp.cos(ec)], axis=-1).astype(dtype)

def dwconv_centred(x, w, b):
    L = x.shape[1]
    xp = jnp.pad(x, ((0, 0), (CONV_W // 2, CONV_W - 1 - CONV_W // 2), (0, 0)))
    out = b
    for k in range(CONV_W):
        out = out + xp[:, k:k + L] * w[k]
    return out

def blockdiag(x, w, b):
    xh = x.reshape(x.shape[0], x.shape[1], RNN_HEADS, RNN_HB)
    return jnp.einsum('blhi,hij->blhj', xh, w).reshape(x.shape) + b

def linear_scan(a, b, h0):
    b = b.at[:, 0].add(a[:, 0] * h0)

    def combine(e1, e2):
        a1, b1 = e1
        a2, b2 = e2
        return a1 * a2, a2 * b1 + b2

    _, h = lax.associative_scan(combine, (a, b), axis=1)
    return h

def rglru_dir(x, wa, ba, wx, bx, lam, h0, reverse):
    xf = x.astype(jnp.float32)
    r = jax.nn.sigmoid(blockdiag(xf, wa.astype(jnp.float32), ba.astype(jnp.float32)))
    i = jax.nn.sigmoid(blockdiag(xf, wx.astype(jnp.float32), bx.astype(jnp.float32)))
    log_a = RG_C * r * jax.nn.log_sigmoid(lam.astype(jnp.float32))
    a = jnp.exp(log_a)
    bterm = jnp.sqrt(-jnp.expm1(2.0 * log_a)) * (i * xf)
    h0f = h0.astype(jnp.float32)
    if reverse:
        h = jnp.flip(linear_scan(jnp.flip(a, 1), jnp.flip(bterm, 1), h0f), 1)
        h_last = h[:, 0]
    else:
        h = linear_scan(a, bterm, h0f)
        h_last = h[:, -1]
    return h.astype(x.dtype), h_last.astype(x.dtype)

def pool_mix(x, pool_w, pool_b, pool_scale):
    B, L, _ = x.shape
    xf = x.astype(jnp.float32)
    cs = jnp.concatenate([jnp.zeros((B, 1, D_POOL), jnp.float32), jnp.cumsum(xf, axis=1)], axis=1)
    t = jnp.arange(L)
    outs = []
    for gi, w in enumerate(POOL_WINDOWS):
        lo = jnp.clip(t - w // 2, 0, L)
        hi = jnp.clip(t + w // 2, 0, L)
        csg = cs[..., gi * POOL_GW:(gi + 1) * POOL_GW]
        cnt = (hi - lo).astype(jnp.float32)[None, :, None]
        outs.append((csg[:, hi] - csg[:, lo]) / cnt)
    pooled = (jnp.concatenate(outs, axis=-1) - xf).astype(x.dtype)
    pg = pooled.reshape(B, L, POOL_GROUPS, POOL_GW)
    y = jnp.einsum('blgi,gij->blgj', pg, pool_w).reshape(B, L, D_POOL) + pool_b
    return y * pool_scale

def mixer(h, w_in, conv_w, conv_b, rg_wa, rg_ba, rg_wx, rg_bx, rg_lambda,
          w_up_rnn, pool_w, pool_b, pool_scale, w_up_pool, w_o, h0f, h0b):
    proj = h @ w_in
    s1, s2, s3, s4 = D_RNN, 2 * D_RNN, 2 * D_RNN + D_POOL, 2 * D_RNN + D_POOL + D_MODEL
    xr, yr, xp, ga, gb = proj[..., :s1], proj[..., s1:s2], proj[..., s2:s3], proj[..., s3:s4], proj[..., s4:]
    xr = dwconv_centred(xr, conv_w, conv_b)
    hf, sf = rglru_dir(xr, rg_wa[0], rg_ba[0], rg_wx[0], rg_bx[0], rg_lambda[0], h0f, False)
    hb, sb = rglru_dir(xr, rg_wa[1], rg_ba[1], rg_wx[1], rg_bx[1], rg_lambda[1], h0b, True)
    branch_a = ((hf + hb) * jax.nn.gelu(yr)) @ w_up_rnn
    branch_b = pool_mix(xp, pool_w, pool_b, pool_scale) @ w_up_pool
    merged = jax.nn.sigmoid(ga) * branch_a + jax.nn.sigmoid(gb) * branch_b
    return merged @ w_o, jnp.stack([sf, sb], axis=1)

def peer(h, wq, keys, u_tab, v_tab):
    B, L, D = h.shape
    T = B * L
    xt = h.reshape(T, D)
    q = (xt @ wq).reshape(T, PEER_HEADS, 2, PEER_DHALF)
    s = jnp.einsum('thpd,hpnd->thpn', q, keys).astype(jnp.float32)
    v1, i1 = lax.top_k(s[:, :, 0], PEER_TOPK)
    v2, i2 = lax.top_k(s[:, :, 1], PEER_TOPK)
    cand = (v1[..., :, None] + v2[..., None, :]).reshape(T, PEER_HEADS, PEER_TOPK * PEER_TOPK)
    sc, ci = lax.top_k(cand, PEER_TOPK)
    e = (jnp.take_along_axis(i1, ci // PEER_TOPK, axis=-1) * N_KEYS
         + jnp.take_along_axis(i2, ci % PEER_TOPK, axis=-1))
    g = jax.nn.softmax(sc, axis=-1).astype(h.dtype)
    nb = T // PEER_BLOCK
    hk = PEER_HEADS * PEER_TOPK

    def block(args):
        xb, eb, gbk = args
        ub = jnp.take(u_tab, eb, axis=0)
        act = jax.nn.gelu(jnp.einsum('cd,ced->ce', xb, ub))
        vb = jnp.take(v_tab, eb, axis=0)
        return jnp.einsum('ce,ced->cd', gbk * act, vb)

    out = lax.map(block, (xt.reshape(nb, PEER_BLOCK, D), e.reshape(nb, PEER_BLOCK, hk),
                          g.reshape(nb, PEER_BLOCK, hk)))
    return out.reshape(B, L, D)

def trunk_layer(x, mod, h0f, h0b, norm1_g, norm2_g, w_in, conv_w, conv_b, rg_wa, rg_ba, rg_wx, rg_bx,
                rg_lambda, w_up_rnn, pool_w, pool_b, pool_scale, w_up_pool, w_o,
                peer_wq, peer_keys, peer_u, peer_v):
    sh1, sc1, g1, sh2, sc2, g2 = jnp.split(mod.astype(x.dtype), 6, axis=-1)
    h = rmsnorm(x, norm1_g) * (1 + sc1) + sh1
    m, st = mixer(h, w_in, conv_w, conv_b, rg_wa, rg_ba, rg_wx, rg_bx, rg_lambda,
                  w_up_rnn, pool_w, pool_b, pool_scale, w_up_pool, w_o, h0f, h0b)
    x = x + g1 * m
    h = rmsnorm(x, norm2_g) * (1 + sc2) + sh2
    x = x + g2 * peer(h, peer_wq, peer_keys, peer_u, peer_v)
    return x, st

def setup_inputs(seed: int = 0) -> dict:
    key = jax.random.key(seed)
    ks = jax.random.split(key, 32)
    f32 = jnp.float32

    def nrm(k, shape, scale):
        return jax.random.normal(k, shape, f32) * scale

    a8 = jax.random.uniform(ks[14], (DEPTH, 2, D_RNN), f32, 0.9, 0.999)
    sig = a8 ** (1.0 / RG_C)
    rg_lambda = jnp.log(sig) - jnp.log1p(-sig)
    return {
        'x_prompt': nrm(ks[0], (BATCH, SEQ, D_MODEL), 1.0),
        'x_sample': nrm(ks[1], (DEC_BATCH, DEC_SEQ, D_MODEL), 1.0),
        'state_rglru': nrm(ks[2], (DEC_BATCH, DEPTH, 2, D_RNN), 0.5),
        'c': nrm(ks[3], (DEC_BATCH, D_MODEL), 1.0),
        'c_ctx': nrm(ks[4], (D_MODEL,), 1.0),
        'norm1_g': 1.0 + nrm(ks[5], (DEPTH, D_MODEL), 0.02),
        'norm2_g': 1.0 + nrm(ks[6], (DEPTH, D_MODEL), 0.02),
        'w_mod': nrm(ks[7], (DEPTH, D_MODEL, 6 * D_MODEL), D_MODEL ** -0.5),
        'b_mod': nrm(ks[8], (DEPTH, 6 * D_MODEL), 0.01),
        'w_in': nrm(ks[9], (DEPTH, D_MODEL, D_IN), D_MODEL ** -0.5),
        'conv_w': nrm(ks[10], (DEPTH, CONV_W, D_RNN), CONV_W ** -0.5),
        'conv_b': nrm(ks[11], (DEPTH, D_RNN), 0.01),
        'rg_wa': nrm(ks[12], (DEPTH, 2, RNN_HEADS, RNN_HB, RNN_HB), RNN_HB ** -0.5),
        'rg_ba': nrm(ks[13], (DEPTH, 2, D_RNN), 0.01),
        'rg_wx': nrm(ks[15], (DEPTH, 2, RNN_HEADS, RNN_HB, RNN_HB), RNN_HB ** -0.5),
        'rg_bx': nrm(ks[16], (DEPTH, 2, D_RNN), 0.01),
        'rg_lambda': rg_lambda,
        'w_up_rnn': nrm(ks[17], (DEPTH, D_RNN, D_MODEL), D_RNN ** -0.5),
        'pool_w': nrm(ks[18], (DEPTH, POOL_GROUPS, POOL_GW, POOL_GW), POOL_GW ** -0.5),
        'pool_b': nrm(ks[19], (DEPTH, D_POOL), 0.01),
        'pool_scale': 1.0 + nrm(ks[20], (DEPTH, D_POOL), 0.02),
        'w_up_pool': nrm(ks[21], (DEPTH, D_POOL, D_MODEL), D_POOL ** -0.5),
        'w_o': nrm(ks[22], (DEPTH, D_MODEL, D_MODEL), D_MODEL ** -0.5),
        'peer_wq': nrm(ks[23], (DEPTH, D_MODEL, PEER_HEADS * PEER_DKEY), D_MODEL ** -0.5),
        'peer_keys': nrm(ks[24], (DEPTH, PEER_HEADS, 2, N_KEYS, PEER_DHALF), PEER_DHALF ** -0.5),
        'peer_u': nrm(ks[25], (DEPTH, N_EXPERTS, D_MODEL), D_MODEL ** -0.5),
        'peer_v': nrm(ks[26], (DEPTH, N_EXPERTS, D_MODEL), 1.0),
        'final_g': 1.0 + nrm(ks[27], (D_MODEL,), 0.02),
    }

def reference(x_prompt, x_sample, state_rglru, c, c_ctx, norm1_g, norm2_g, w_mod, b_mod, w_in,
              conv_w, conv_b, rg_wa, rg_ba, rg_wx, rg_bx, rg_lambda, w_up_rnn, pool_w, pool_b,
              pool_scale, w_up_pool, w_o, peer_wq, peer_keys, peer_u, peer_v, final_g):
    xc = x_prompt
    xs = x_sample + grid_pos_embed(x_sample.shape[1], x_sample.dtype)[None]
    new_states = []
    for l in range(DEPTH):
        mod_ctx = (jax.nn.silu(c_ctx) @ w_mod[l] + b_mod[l])[None, None, :]
        mod_lat = (jax.nn.silu(c) @ w_mod[l] + b_mod[l])[:, None, :]
        h0 = jnp.zeros((xc.shape[0], D_RNN), xc.dtype)
        xc, st = trunk_layer(xc, mod_ctx, h0, h0, norm1_g[l], norm2_g[l], w_in[l], conv_w[l], conv_b[l],
                             rg_wa[l], rg_ba[l], rg_wx[l], rg_bx[l], rg_lambda[l], w_up_rnn[l], pool_w[l],
                             pool_b[l], pool_scale[l], w_up_pool[l], w_o[l], peer_wq[l], peer_keys[l],
                             peer_u[l], peer_v[l])
        new_states.append(st)
        xs, _ = trunk_layer(xs, mod_lat, state_rglru[:, l, 0], state_rglru[:, l, 1], norm1_g[l], norm2_g[l],
                            w_in[l], conv_w[l], conv_b[l], rg_wa[l], rg_ba[l], rg_wx[l], rg_bx[l],
                            rg_lambda[l], w_up_rnn[l], pool_w[l], pool_b[l], pool_scale[l], w_up_pool[l],
                            w_o[l], peer_wq[l], peer_keys[l], peer_u[l], peer_v[l])
    y_prompt = rmsnorm(xc, final_g)
    y_sample = rmsnorm(xs, final_g)
    new_state_rglru = jnp.stack(new_states, axis=1)
    return (y_prompt, y_sample, new_state_rglru)


_drawn_inputs = setup_inputs


def setup_inputs(seed=0):
    import zlib

    import numpy as np

    out = dict(_drawn_inputs(seed))
    spreads = {}
    factors = {'rg_ba': 32.162,
     'rg_bx': 16.334,
     'pool_b': 4.361,
     'pool_scale': 3.482,
     'final_g': 29.426,
     'conv_b': 2.73}
    for name, (base, spread) in spreads.items():
        noise = np.random.default_rng([zlib.crc32(name.encode()), seed]).standard_normal(out[name].shape)
        drawn = base * np.exp(spread * noise) if base else spread * noise
        out[name] = __import__('jax').numpy.asarray(drawn.astype(out[name].dtype))
    for name, factor in factors.items():
        out[name] = (out[name] * factor).astype(out[name].dtype)
    return out
```

```python
import concourse.bass as bass
from concourse import mybir

D = 1024
KC = D // 128
TA, TB = 128, 512
T = TA + TB
HALF = T // 2
NT = T // 128
HEADS, TOPK, NKEY = 8, 16, 128
SLOTS = HEADS * TOPK
EPS = 1e-6
RAW, SPL, SBANKS = 4, 2, 2
GAP = 3
W = TA + GAP + TB + 1
WH = W // 2
PADX = 16
PW = PADX + TA + PADX + TB + PADX
BIG = -3.0e38
UR = 4

V_N1, V_N2, V_BMOD, V_CW, V_CB, V_BA, V_BX, V_LAM, V_PB, V_PS, V_FG, V_ST, V_END = (
    0, 8, 16, 64, 96, 104, 120, 136, 152, 156, 160, 168, 184)

B_MOD1, B_XP, B_XR, B_YR, B_MIX, B_G1, B_WO, B_MOD2, B_WQ, B_G2, NB = (
    0, 16, 20, 28, 36, 68, 76, 84, 100, 116, 124)
P_XP, P_XR, P_YR, P_MIX, P_WO, P_WQ, P_END = 0, 4, 12, 20, 52, 60, 76
S_H1, S_PB, S_A, S_MG, S_H2, S_END = 0, 8, 12, 20, 28, 36


def hold(eng, sem, value, settled):
    eng.wait_ge(sem, value)
    eng.sem_inc(settled, 1)


class Chain:

    def __init__(self, eng, sem, settled):
        self.eng, self.sem, self.settled, self.total, self.base, self.n, self.looping = eng, sem, settled, 0, 0, 0, False

    def enter(self, i, per):
        if not self.looping:
            self.total, self.looping = self.total + self.n, True
        self.base, self.n, self.per = i * per + self.total, 0, per

    def leave(self, times):
        assert self.n == self.per, (self.n, self.per)
        self.total += times * self.per
        self.base, self.n, self.looping = self.total, 0, False

    def link(self, ins):
        ins.then_inc(self.sem, 1)
        self.n += 1

    def wait(self):
        if isinstance(self.base, int):
            self.eng.wait_ge(self.sem, self.base + self.n)
        else:
            hold(self.eng, self.sem, self.base + self.n, self.settled)

    def step(self, ins):
        self.link(ins)
        self.wait()


def build(nc, xT, posT, cT, vecs_d, iota_d, invc_d, gw_d, pw_d, keys_d, wblk, u_tab, v_tab, ident_d, yT, st_out):
    f32, f32r, u32 = mybir.dt.float32, mybir.dt.float32r, mybir.dt.uint32
    ALU, ACT, AX = mybir.AluOpType, mybir.ActivationFunctionType, mybir.AxisListType
    ds = bass.ds

    keep = []

    def sb(name, shape, dt=f32):
        g = nc.sbuf_tensor(name, shape, dt)
        t = g.__enter__()
        keep.append(g)
        return t

    def free_to(mark):
        while len(keep) > mark:
            keep.pop().__exit__(None, None, None)

    def sem(name):
        return nc.semaphore(name).__enter__()

    x = sb("x", [128, KC, T])
    hs = sb("hs", [128, KC, T])
    hHi = sb("hHi", [128, KC, T], f32r)
    hLo = sb("hLo", [128, KC, T], f32r)
    raw = sb("raw", [128, RAW, D])
    wHi = sb("wHi", [128, SPL, D], f32r)
    wLo = sb("wLo", [128, SPL, D], f32r)
    vecs = sb("vecs", [128, V_END])
    keysT = sb("keysT", [128, 16, NKEY])
    ident = sb("ident", [128, 128])
    ones = sb("ones", [128, 128])
    iota16 = sb("iota16", [128, 16])
    cvec = sb("cvec", [128, KC * 2])
    csig = sb("csig", [128, KC * 2])
    mod = sb("mod", [128, 48, 2])
    scl1 = sb("scl1", [128, KC, 2])
    scl2 = sb("scl2", [128, KC, 2])
    sq = sb("sq", [128, 2, T])
    rstd = sb("rstd", [128, T])
    stfin = sb("stfin", [128, 2, KC])
    sp = sb("sp", [128, 16])
    sp4 = sb("sp4", [128, 16])
    spt = sb("spt", [128, 4, 16])
    base_mark = len(keep)
    pbHi = sb("pbHi", [128, 4, T], f32r)
    pbLo = sb("pbLo", [128, 4, T], f32r)
    mix_mark = len(keep)
    gw = sb("gw", [128, 32, 128])
    poolw = sb("poolw", [128, 4, 128])
    rec_mark = len(keep)
    invc = sb("invc", [128, 4, T])
    px = sb("px", [128, PW])
    ps1 = sb("ps1", [128, PW])
    ps2 = sb("ps2", [128, PW])
    pooled = sb("pooled", [128, T])
    pyf = sb("pyf", [128, T])
    pbias = sb("pbias", [128, 4])
    free_to(rec_mark)
    xrp = sb("xrp", [128, 2, W + 3])
    xc = sb("xc", [128, 2, W])
    gr = [sb(f"gr{d}", [128, 2, WH]) for d in range(2)]
    gi = [sb(f"gi{d}", [128, 2, WH]) for d in range(2)]
    gs = [sb(f"gs{d}", [128, 2, WH]) for d in range(2)]
    gq = sb("gq", [128, W])
    hdir = [sb(f"hdir{d}", [128, W]) for d in range(2)]
    free_to(mix_mark)
    aHi = sb("aHi", [128, KC, T], f32r)
    aLo = sb("aLo", [128, KC, T], f32r)
    gy = sb("gy", [128, 2, T])
    sga = gy
    sgb = sb("sgb", [128, 2, T])
    tm1, tm2 = sq[:, 0, :], sq[:, 1, :]
    free_to(base_mark)
    qf = [sb(f"qf{d}", [128, T]) for d in range(2)]
    S = sb("S", [128, 4, NT * NKEY])
    v8 = sb("v8", [128, 2, TOPK])
    i8 = sb("i8", [128, 2, TOPK], u32)
    cand = sb("cand", [128, TOPK * TOPK])
    sw = sb("sw", [128, 2, NKEY])
    s16 = sb("s16", [128, TOPK])
    c16 = sb("c16", [128, TOPK], u32)
    i1f = sb("i1f", [128, 2, NT * TOPK])
    ab = sb("ab", [128, 2, NT * TOPK], u32)
    abf = sb("abf", [128, 2, NT * TOPK])
    CI = sb("CI", [128, NT * TOPK], u32)
    oh = sb("oh", [128, 2, NT * TOPK * TOPK])
    esel = abf
    SC = sb("SC", [128, NT * SLOTS])
    SCm = sb("SCm", [128, NT * SLOTS])
    den = sb("den", [128, NT * HEADS])
    E = sb("E", [128, NT * SLOTS], u32)
    Eg = sb("Eg", [128, 2, UR], u32)
    htok = sb("htok", [128, NT, D])
    rows = sb("rows", [128, UR, D])
    accB = oh[:, 1, 0:D]
    actv = sb("actv", [128, NT * SLOTS])
    wgt = SCm
    acc = htok

    P = [nc.psum_tensor(f"P{b}", [128, 2, 512], f32).__enter__() for b in range(4)]

    names = ("x_ld small_ld x_ready ones_ready csig_ready c_ready sq_done sq_used ssq_done ms_ready std_ready norm_t hF_ready hi_ready "
             "lo_ready prod_done split_free xpp_ready pooled_ready poolmm_done py_ready sp_e sp_ready "
             "conv_done gates_done sig_done gates_act dir_done hsum_ready gy_ready a_ready sgb_ready merged_ready "
             "x2_ready qf_ready score_done S_ready head_done scm_ready exp_ready tr_done htok_ready "
             "e_ready row_free act_ready gel_ready wgt_ready acc_ready accT_done x3_ready "
             "y_ready y_st st_st st_ready sel_c dve_c act_c pool_c mod_ready pool_held dve_held eg_ready acc_c").split()
    s = {n: sem(n) for n in names}
    raw_ld = [sem(f"raw_ld{j}") for j in range(RAW)]
    raw_used = [sem(f"raw_used{j}") for j in range(RAW)]
    psum_free = [sem(f"psum_free{j}") for j in range(4)]
    row_ld = [sem(f"row_ld{j}") for j in range(UR)]
    block = nc.Block().__enter__()

    def col(j):
        return vecs[:, j:j + 1]

    def vcol(j, n=1):
        return vecs[:, ds(j, n)]

    NSMALL = 9

    @block.sync
    def _(sp_):
        sp_.dma_start(x[:, :, :], xT).then_inc(s["x_ld"], 16)
        for dst, src in ((hs[:, :, 0:TB], posT), (cvec[:, :], cT), (vecs[:, :], vecs_d), (iota16[:, :], iota_d),
                         (gw[:, :, :], gw_d), (poolw[:, :, :], pw_d), (invc[:, :, :], invc_d),
                         (keysT[:, :, :], keys_d), (ident[:, :], ident_d)):
            sp_.dma_start(dst, src).then_inc(s["small_ld"], 16)
        for j in range(RAW):
            sp_.dma_start(raw[:, j, :], wblk[j, :, :]).then_inc(raw_ld[j], 16)
        with sp_.Fori(1, NB // RAW) as i:
            for j in range(RAW):
                sp_.wait_ge(raw_used[j], i)
                sp_.dma_start(raw[:, j, :], wblk[ds(i * RAW + j, 1), :, :].rearrange("a p n -> (a p) n")
                              ).then_inc(raw_ld[j], 16)
        sp_.wait_ge(s["st_ready"], 1)
        sp_.dma_start(st_out, stfin[:, :, :]).then_inc(s["st_st"], 16)
        sp_.wait_ge(s["y_ready"], KC)
        sp_.dma_start(yT, hs[:, :, :]).then_inc(s["y_st"], 16)
        sp_.wait_ge(s["st_st"], 16)
        sp_.wait_ge(s["y_st"], 16)

    @block.gpsimd
    def _(pool):
        def split(i, blk, prod):
            for j in range(4):
                pool.wait_ge(raw_ld[j], (i + blk // 4 + 1) * 16)
                if prod + j >= SPL:
                    pool.wait_ge(s["prod_done"], i * 4 + (prod + j - SPL + 1))
                pool.sem_inc(s["pool_held"], 1)
                pool.tensor_copy(wHi[:, j % 2, :], raw[:, j, :]).then_inc(s["pool_c"], 1)
                pool.wait_ge(s["pool_c"], i * 4 + (prod + j + 1))
                pool.tensor_tensor(wLo[:, j % 2, :], raw[:, j, :], wHi[:, j % 2, :].bitcast(f32),
                                   ALU.subtract).then_inc(raw_used[j], 1)

        def splits(blk, prod, n):
            if n > 4:
                with pool.Fori(0, n // 4) as i:
                    split(i, blk, prod)
            else:
                split(0, blk, prod)

        split(0, B_XP, P_XP)
        splits(B_XR, P_XR, B_G1 - B_XR)
        splits(B_WO, P_WO, 8)
        splits(B_WQ, P_WQ, 16)

        pool.wait_ge(s["e_ready"], 1)
        with pool.Fori(0, NT) as t:
            for which, tab in ((0, u_tab), (1, v_tab)):
                with pool.Fori(0, SLOTS // (2 * UR)) as g:
                    for b in range(2):
                        pool.tensor_copy(Eg[:, b, :], E[:, ds(t * SLOTS + g * (2 * UR) + b * UR, UR)]
                                         ).then_inc(s["eg_ready"], 1)
                        hold(pool, s["eg_ready"], t * (2 * SLOTS // UR) + g * 2 + (which * SLOTS // UR + b + 1),
                             s["pool_held"])
                        for j in range(UR):
                            hold(pool, s["row_free"], t * (2 * SLOTS) + g * (2 * UR)
                                 + (which * SLOTS + b * UR + j + 1), s["pool_held"])
                            pool.indirect_dma_start(
                                out=rows[:, j, :], out_offset=None, in_=tab,
                                in_offset=bass.IndirectOffsetOnAxis(ap=Eg[:, b, j:j + 1], axis=0),
                            ).then_inc(row_ld[j], 16)

    @block.tensor
    def _(pe):
        def cols(t2, k, h):
            return t2[:, k, h * HALF:(h + 1) * HALF]

        def product(i, blk, prod, pslot, prior, hi, lo, kk=KC, per=2, lo_at=None):
            j, sl = blk % 4, prod % 2
            pe.wait_ge(raw_used[j], i + (blk // 4 + 1))
            if prior is not None:
                pe.wait_ge(psum_free[pslot], prior)
            for k in range(kk):
                st = (k == 0)
                for a, (w_, xs) in enumerate(((wHi, (hi, lo)), (wLo, (hi,)))):
                    for b, x_ in enumerate(xs):
                        for h in range(2):
                            last = nc.tensor.matmul(P[pslot][:, h, 0:HALF], w_[:, sl, k * 128:(k + 1) * 128],
                                                    cols(x_, k, h), start=(st and a == 0 and b == 0),
                                                    stop=(k == kk - 1 and a == 1))
            return last

        def norm_sum(n):
            for k in range(KC):
                pe.wait_ge(s["sq_done"], n * KC + k + 1)
                for h in range(2):
                    last = nc.tensor.matmul(P[2][:, h, 0:HALF], ones[:, :], sq[:, k % 2, h * HALF:(h + 1) * HALF],
                                            start=(k == 0), stop=(k == KC - 1))
                last.then_inc(s["sq_used"], 1)

        def modulation(blk, m0, n):
            with pe.Fori(0, n // 4) as i:
                for j in range(4):
                    pe.wait_ge(raw_ld[j], (i + blk // 4 + 1) * 16)
                    for k in range(KC):
                        last = nc.tensor.matmul(P[3][:, 1, ds((i * 4 + m0 + j) * 2, 2)],
                                                raw[:, j, k * 128:(k + 1) * 128],
                                                cvec[:, 2 * k:2 * k + 2], start=(k == 0), stop=(k == KC - 1))
                    last.then_inc(raw_used[j], 1)

        pe.wait_ge(s["ones_ready"], 1)
        pe.wait_ge(s["c_ready"], 1)
        norm_sum(0)
        modulation(B_MOD1, 0, 16)
        pe.wait_ge(s["lo_ready"], S_PB)
        for m in range(5):
            if m < 4:
                product(0, B_XP + m, P_XP + m, m % 2, m // 2 if m > 1 else None, hHi, hLo).then_inc(s["prod_done"], 1)
            if m > 0:
                pe.wait_ge(s["pooled_ready"], m)
                if m > 1:
                    pe.wait_ge(s["py_ready"], m - 1)
                for h in range(2):
                    last = nc.tensor.matmul(P[2][:, h, 0:HALF], poolw[:, m - 1, :],
                                            pooled[:, h * HALF:(h + 1) * HALF], start=True, stop=True)
                last.then_inc(s["poolmm_done"], 1)

        def gates(m, d):
            if d == 0:
                pe.wait_ge(s["conv_done"], m + 1)
            if m or d:
                pe.wait_ge(s["sig_done"], 2 * m + d)
            for kind in range(2):
                for h in range(2):
                    last = nc.tensor.matmul(P[2 + kind][:, h, 0:WH], gw[:, (d * 2 + kind) * 8 + m, :],
                                            xc[:, m % 2, h * WH:(h + 1) * WH], start=True, stop=True)
            last.then_inc(s["gates_done"], 1)

        for m in range(KC + 1):
            if m > 0:
                gates(m - 1, 0)
            pr = P_XR + m
            product(0, B_XR + m, pr, pr % 2, pr // 2, hHi, hLo).then_inc(s["prod_done"], 1)
            if m > 0:
                gates(m - 1, 1)
        for m in range(1, KC):
            pr = P_YR + m
            product(0, B_YR + m, pr, pr % 2, pr // 2, hHi, hLo).then_inc(s["prod_done"], 1)
        pe.wait_ge(s["sig_done"], 2 * KC)

        def mix(m):
            for j, (hi, lo, kk) in enumerate(((hHi, hLo, 8), (aHi, aLo, 8), (hHi, hLo, 8), (pbHi, pbLo, 4))):
                if j == 1:
                    pe.wait_ge(s["lo_ready"], S_MG)
                product(m, B_MIX + j, P_MIX + j, j, m + (10 if j < 2 else 0), hi, lo, kk).then_inc(s["prod_done"], 1)

        with pe.Fori(0, KC) as m:
            mix(m)
        pe.wait_ge(s["merged_ready"], KC)
        modulation(B_G1, 16, 8)
        pe.wait_ge(s["lo_ready"], S_H2)
        with pe.Fori(0, 2) as i:
            for j in range(4):
                product(i, B_WO + j, P_WO + j, j % 2, i * 2 + (18 + j // 2), hHi, hLo).then_inc(s["prod_done"], 1)
        norm_sum(1)
        modulation(B_MOD2, 24, 16)
        pe.wait_ge(s["lo_ready"], S_END)

        def scores(i, j):
            pe.wait_ge(psum_free[j % 2], i * 2 + (22 + j // 2 + 1))
            pr = 2 + j % 2
            if i * 4 + j >= 2:
                pe.wait_ge(s["S_ready"], i * 4 + j - 1)
            for t in range(NT):
                last = nc.tensor.matmul(P[pr][:, t // 4, (t % 4) * 128:(t % 4 + 1) * 128],
                                        qf[j % 2][:, t * 128:(t + 1) * 128],
                                        keysT[:, ds(i * 4 + j, 1), :].rearrange("p a n -> p (a n)"),
                                        start=True, stop=True)
            last.then_inc(s["score_done"], 1)

        def qprod(i, j):
            jj = j % 4
            product(i if j < 4 else i + 1, B_WQ + jj, P_WQ + jj, j % 2, i * 2 + (22 + j // 2), hHi, hLo
                    ).then_inc(s["prod_done"], 1)

        qprod(0, 0)
        for i in range(4):
            for j in range(4):
                if i * 4 + j < 15:
                    qprod(i, j + 1)
                scores(i, j)
        pe.wait_ge(s["S_ready"], 16)
        for t in range(NT):
            if t >= 2:
                pe.wait_ge(s["htok_ready"], t - 1)
            for k in range(KC):
                last = nc.tensor.transpose(P[2 + t % 2][:, k // 4, (k % 4) * 128:(k % 4 + 1) * 128],
                                           hs[:, k, t * 128:(t + 1) * 128], ident[:, :])
            last.then_inc(s["tr_done"], 1)
        pe.wait_ge(s["htok_ready"], NT)
        modulation(B_G2, 40, 8)
        for t in range(NT):
            pe.wait_ge(s["acc_ready"], t + 1)
            if t == 0:
                pe.wait_ge(psum_free[0], 30)
                pe.wait_ge(s["htok_ready"], NT)
            if t >= 2:
                pe.wait_ge(s["x3_ready"], t - 1)
            for k in range(KC):
                last = nc.tensor.transpose(P[(t % 2) * 2][:, k // 4, (k % 4) * 128:(k % 4 + 1) * 128],
                                           acc[:, t, k * 128:(k + 1) * 128], ident[:, :])
            last.then_inc(s["accT_done"], 1)
        pe.wait_ge(s["x3_ready"], NT)
        norm_sum(2)

    @block.scalar
    def _(act):
        def actf(out, in_, f, **kw):
            return nc.scalar.activation(out, in_, f, **kw)

        def squares(n):
            for k in range(KC):
                c = n * KC + k
                if n == 1:
                    act.wait_ge(psum_free[k % 2], 18 + k // 2 + 1)
                if c >= 2:
                    act.wait_ge(s["sq_used"], c - 1)
                actf(sq[:, k % 2, :], x[:, k, :], ACT.Square).then_inc(s["sq_done"], 1)

        def his(n0, n, dst, src, ready, r0):
            with act.Fori(0, n) as k:
                act.wait_ge(ready, k + (r0 + 1))
                actf(dst[:, ds(k, 1), :], src[:, ds(k, 1), :], ACT.Copy).then_inc(s["hi_ready"], 1)

        def normed(n, scl, sh0):
            act.wait_ge(s["ms_ready"], n + 1)
            actf(rstd[:, :], rstd[:, :], ACT.Sqrt).then_inc(s["std_ready"], 1)
            if scl is None:
                return
            act.wait_ge(s["mod_ready"], n + 1)
            with act.Fori(0, KC) as k:
                act.wait_ge(s["norm_t"], k + (n * KC + 1))
                hk = hs[:, ds(k, 1), :].rearrange("p a n -> p (a n)")
                for g, (c0, c1) in enumerate(((0, TA), (TA, T))):
                    last = actf(hk[:, c0:c1], hk[:, c0:c1], ACT.Identity,
                                scale=scl[:, ds(k, 1), g:g + 1].rearrange("p a n -> p (a n)"),
                                bias=mod[:, ds(k + sh0, 1), g:g + 1].rearrange("p a n -> p (a n)"))
                last.then_inc(s["hF_ready"], 1)
                act.wait_ge(s["hF_ready"], k + (n * KC + 1))
                actf(hHi[:, ds(k, 1), :], hs[:, ds(k, 1), :], ACT.Copy).then_inc(s["hi_ready"], 1)

        act.wait_ge(s["small_ld"], 16 * NSMALL)
        actf(csig[:, :], cvec[:, :], ACT.Sigmoid).then_inc(s["csig_ready"], 1)
        act.wait_ge(s["sp_e"], 1)
        actf(spt[:, 0, :], spt[:, 0, :], ACT.Exp).then_inc(s["act_c"], 1)
        act.wait_ge(s["x_ready"], 1)
        squares(0)
        normed(0, scl1, 0)
        for m in range(4):
            act.wait_ge(s["prod_done"], m + 1)
            if m >= 1:
                act.wait_ge(s["pooled_ready"], m)
            for (c0, c1, o) in ((0, TA, PADX), (TA, HALF, 2 * PADX), (HALF, T, 2 * PADX)):
                h = c0 // HALF
                last = actf(px[:, c0 + o:c1 + o], P[m % 2][:, h, c0 - h * HALF:c1 - h * HALF], ACT.Copy)
            last.then_inc(psum_free[m % 2], 1)
            act.wait_ge(s["poolmm_done"], m + 1)
            actf(pyf[:, :].rearrange("p (h n) -> p h n", h=2), P[2][:, :, 0:HALF], ACT.Identity,
                 scale=col(V_PS + m), bias=pbias[:, m:m + 1]).then_inc(s["py_ready"], 1)
            act.wait_ge(s["py_ready"], m + 1)
            actf(pbHi[:, m, :], pyf[:, :], ACT.Copy).then_inc(s["hi_ready"], 1)

        def xr_out(m):
            act.wait_ge(s["prod_done"], P_XR + m + 1)
            if m >= 2:
                act.wait_ge(s["conv_done"], m - 1)
            for (c0, c1, o) in ((0, TA, 2), (TA, HALF, 2 + GAP), (HALF, T, 2 + GAP)):
                h = c0 // HALF
                last = actf(xrp[:, m % 2, c0 + o:c1 + o], P[m % 2][:, h, c0 - h * HALF:c1 - h * HALF], ACT.Copy)
            last.then_inc(psum_free[m % 2], 1)

        def sigs(m, d):
            act.wait_ge(s["gates_done"], 2 * m + d + 1)
            if m >= 1:
                act.wait_ge(s["dir_done"], 2 * (m - 1) + d + 1)
            actf(gr[d][:, :, :], P[2][:, :, 0:WH], ACT.Sigmoid, bias=col(V_BA + d * 8 + m)).then_inc(s["act_c"], 1)
            actf(gi[d][:, :, :], P[3][:, :, 0:WH], ACT.Sigmoid, bias=col(V_BX + d * 8 + m)).then_inc(s["sig_done"], 1)

        act.wait_ge(s["sp_ready"], 1)
        act.wait_ge(s["xpp_ready"], 2)
        xr_out(0)
        for m in range(KC):
            sigs(m, 0)
            if m + 1 < KC:
                xr_out(m + 1)
            sigs(m, 1)
            act.wait_ge(s["act_c"], 1 + 4 * m + 2)
            for d in range(2):
                actf(gr[d][:, :, :], gr[d][:, :, :], ACT.Tanh, scale=sp4[:, d * 8 + m:d * 8 + m + 1]
                     ).then_inc(s["act_c"], 1)
            act.wait_ge(s["act_c"], 1 + 4 * m + 4)
            for d in range(2):
                actf(gs[d][:, :, :], gr[d][:, :, :], ACT.Sqrt).then_inc(s["gates_act"], 1)
        act.wait_ge(s["dir_done"], 2 * KC)
        for m in range(KC):
            act.wait_ge(s["prod_done"], P_YR + m + 1)
            if m >= 2:
                act.wait_ge(s["a_ready"], m - 1)
            actf(gy[:, m % 2, :].rearrange("p (h n) -> p h n", h=2), P[m % 2][:, :, 0:HALF],
                 ACT.Gelu_apprx_tanh).then_inc(psum_free[m % 2], 1)
        his(S_A, KC, aHi, hs, s["a_ready"], 0)

        with act.Fori(0, KC // 2) as i:
            for b in range(2):
                act.wait_ge(s["prod_done"], (i * 2 + b) * 4 + (P_MIX + 1))
                if b:
                    act.wait_ge(s["merged_ready"], i * 2 + b)
                actf(sga[:, b, :].rearrange("p (h n) -> p h n", h=2), P[0][:, :, 0:HALF], ACT.Sigmoid
                     ).then_inc(psum_free[0], 1)
                act.wait_ge(s["prod_done"], (i * 2 + b) * 4 + (P_MIX + 3))
                actf(sgb[:, b, :].rearrange("p (h n) -> p h n", h=2), P[2][:, :, 0:HALF], ACT.Sigmoid
                     ).then_inc(psum_free[2], 1)
        act.wait_ge(s["prod_done"], P_WO)
        his(S_MG, KC, hHi, hs, s["merged_ready"], 0)
        squares(1)
        normed(1, scl2, 24)

        def q_out(j):
            act.wait_ge(s["prod_done"], P_WQ + j + 1)
            if j >= 2:
                act.wait_ge(s["score_done"], j - 1)
            actf(qf[j % 2][:, :].rearrange("p (h n) -> p h n", h=2), P[j % 2][:, :, 0:HALF], ACT.Copy
                 ).then_inc(psum_free[j % 2], 1)

        def s_out(j):
            act.wait_ge(s["score_done"], j + 1)
            if j >= 4:
                act.wait_ge(s["head_done"], (j - 4) // 2 + 1)
            pr = 2 + j % 2
            actf(S[:, j % 4, 0:512], P[pr][:, 0, :], ACT.Copy)
            actf(S[:, j % 4, 512:640], P[pr][:, 1, 0:128], ACT.Copy).then_inc(s["S_ready"], 1)

        q_out(0)
        for j in range(16):
            if j < 15:
                q_out(j + 1)
            s_out(j)
        for t in range(NT):
            act.wait_ge(s["tr_done"], t + 1)
            actf(htok[:, t, :].rearrange("p (h n) -> p h n", h=2), P[2 + t % 2][:, :, :], ACT.Copy
                 ).then_inc(s["htok_ready"], 1)
        act.wait_ge(s["scm_ready"], 1)
        actf(SC[:, :], SCm[:, :], ACT.Exp).then_inc(s["exp_ready"], 1)
        for t in range(NT):
            act.wait_ge(s["act_ready"], t + 1)
            actf(wgt[:, t * SLOTS:(t + 1) * SLOTS], actv[:, t * SLOTS:(t + 1) * SLOTS], ACT.Gelu_apprx_tanh
                 ).then_inc(s["gel_ready"], 1)
        act.wait_ge(s["x3_ready"], NT)
        squares(2)
        normed(2, None, 0)

    @block.vector
    def _(dve):
        V = nc.vector
        ch = Chain(dve, s["dve_c"], s["dve_held"])

        def los(n0, n, dst, hi, src):
            with dve.Fori(0, n) as k:
                dve.wait_ge(s["hi_ready"], k + (n0 + 1))
                V.tensor_tensor(dst[:, ds(k, 1), :], src[:, ds(k, 1), :], hi[:, ds(k, 1), :].bitcast(f32),
                                ALU.subtract).then_inc(s["lo_ready"], 1)

        def mods(n, blk, m0, cnt):
            dve.wait_ge(raw_used[3], (blk + cnt) // 4)
            for g in range(2):
                ch.link(V.tensor_tensor(mod[:, m0:m0 + cnt, g], P[3][:, 1, 2 * m0 + g:2 * (m0 + cnt):2],
                                        vecs[:, V_BMOD + m0:V_BMOD + m0 + cnt], ALU.add))
            ch.wait()

        def scale(dst, m_sc, vg, ready):
            for g in range(2):
                last = V.scalar_tensor_tensor(out=dst[:, :, g], in0=mod[:, m_sc:m_sc + KC, g], scalar=1.0,
                                              in1=vecs[:, vg:vg + KC], op0=ALU.add, op1=ALU.mult)
            last.then_inc(ready, 1)

        def inv_rms(n):
            dve.wait_ge(s["sq_used"], (n + 1) * KC)
            V.tensor_scalar(rstd[:, :].rearrange("p (h n) -> p h n", h=2), P[2][:, :, 0:HALF], 1.0 / D, EPS,
                            ALU.mult, ALU.add).then_inc(s["ms_ready"], 1)
            dve.wait_ge(s["std_ready"], n + 1)
            ch.step(V.reciprocal(rstd[:, :], rstd[:, :]))

        def normed(n):
            with dve.Fori(0, KC) as k:
                V.tensor_tensor(hs[:, ds(k, 1), :].rearrange("p a n -> p (a n)"),
                                x[:, ds(k, 1), :].rearrange("p a n -> p (a n)"), rstd[:, :], ALU.mult
                                ).then_inc(s["norm_t"], 1)

        V.memset(ones[:, :], 1.0).then_inc(s["ones_ready"], 1)
        ch.link(V.memset(spt[:, 2, :], 0.0))
        dve.wait_ge(s["small_ld"], 16 * NSMALL)
        dve.wait_ge(s["x_ld"], 16)
        V.tensor_tensor(x[:, :, TA:T], x[:, :, TA:T], hs[:, :, 0:TB], ALU.add).then_inc(s["x_ready"], 1)
        dve.wait_ge(s["csig_ready"], 1)
        V.tensor_tensor(cvec[:, :], cvec[:, :], csig[:, :], ALU.mult).then_inc(s["c_ready"], 1)
        lam = vecs[:, V_LAM:V_LAM + 16]
        ch.step(V.tensor_scalar(spt[:, 0, :], lam, -1.0, None, ALU.mult))
        ch.step(V.tensor_tensor(sp[:, :], spt[:, 0, :], lam, ALU.min))
        V.tensor_copy(spt[:, 0, :], sp[:, :]).then_inc(s["sp_e"], 1)
        dve.wait_ge(s["act_c"], 1)
        e_, z_, z2 = spt[:, 0, :], spt[:, 1, :], spt[:, 3, :]
        ch.step(V.tensor_scalar(z_, e_, 2.0, None, ALU.add))
        ch.step(V.reciprocal(z_, z_))
        ch.step(V.tensor_tensor(z_, z_, e_, ALU.mult))
        ch.step(V.tensor_tensor(z2, z_, z_, ALU.mult))
        ch.step(V.tensor_scalar(e_, z2, 1.0 / 17.0, 1.0 / 15.0, ALU.mult, ALU.add))
        for n in (13, 11, 9, 7, 5, 3, 1):
            ch.step(V.tensor_tensor(e_, e_, z2, ALU.mult))
            ch.step(V.tensor_scalar(e_, e_, 1.0 / n, None, ALU.add))
        ch.step(V.tensor_tensor(e_, e_, z_, ALU.mult))
        ch.step(V.tensor_scalar(z_, lam, -1.0, 0.0, ALU.mult, ALU.max))
        ch.step(V.scalar_tensor_tensor(out=sp[:, :], in0=e_, scalar=2.0, in1=z_, op0=ALU.mult, op1=ALU.add))
        V.tensor_scalar(sp4[:, :], sp[:, :], 4.0, None, ALU.mult).then_inc(s["sp_ready"], 1)
        V.tensor_tensor(pbias[:, :], vecs[:, V_PB:V_PB + 4], vecs[:, V_PS:V_PS + 4], ALU.mult)
        V.memset(px[:, :], 0.0).then_inc(s["xpp_ready"], 1)
        inv_rms(0)
        mods(0, B_MOD1, 0, 16)
        scale(scl1, 8, V_N1, s["mod_ready"])
        normed(0)
        los(S_H1, KC, hLo, hHi, hs)
        for m in range(4):
            dve.wait_ge(psum_free[m % 2], m // 2 + 1)
            src, dst = px, ps1
            step = 0
            for lev in range(m + 1):
                a, b = (1, 0) if lev == 0 else (1 << (lev - 1), 1 << (lev - 1))
                if lev == 0:
                    ch.step(V.tensor_tensor(ps1[:, 1:PW], px[:, 0:PW - 1], px[:, 1:PW], ALU.add))
                    lo_, hi_ = 1, PW
                    src, dst = ps1, ps2
                else:
                    ch.step(V.tensor_tensor(dst[:, lo_ + a:hi_ - b], src[:, lo_:hi_ - a - b],
                                            src[:, lo_ + a + b:hi_], ALU.add))
                    lo_, hi_ = lo_ + a, hi_ - b
                    src, dst = dst, src
            if m >= 1:
                dve.wait_ge(s["poolmm_done"], m)
            for (c0, c1, o) in ((0, TA, PADX), (TA, T, 2 * PADX)):
                ch.link(V.tensor_tensor(pooled[:, c0:c1], src[:, c0 + o:c1 + o], invc[:, m, c0:c1], ALU.mult))
            ch.wait()
            for (c0, c1, o) in ((0, TA, PADX), (TA, T, 2 * PADX)):
                last = V.tensor_tensor(pooled[:, c0:c1], pooled[:, c0:c1], px[:, c0 + o:c1 + o], ALU.subtract)
            last.then_inc(s["pooled_ready"], 1)
            dve.wait_ge(s["hi_ready"], S_PB + m + 1)
            V.tensor_tensor(pbLo[:, m, :], pyf[:, :], pbHi[:, m, :].bitcast(f32), ALU.subtract
                            ).then_inc(s["lo_ready"], 1)
            dve.wait_ge(s["lo_ready"], S_PB + m + 1)
        V.memset(xrp[:, :, :], 0.0).then_inc(s["xpp_ready"], 1)

        def conv(m):
            dve.wait_ge(psum_free[m % 2], P_XR // 2 + m // 2 + 1)
            if m >= 2:
                dve.wait_ge(s["gates_done"], 2 * (m - 1))
            o = xc[:, m % 2, :]
            ch.step(V.tensor_scalar(o, xrp[:, m % 2, 0:W], col(V_CW + m), col(V_CB + m), ALU.mult, ALU.add))
            for k in range(1, 4):
                ins = V.scalar_tensor_tensor(out=o, in0=xrp[:, m % 2, k:k + W], scalar=col(V_CW + 8 * k + m), in1=o,
                                             op0=ALU.mult, op1=ALU.add)
                if k < 3:
                    ch.step(ins)
            ins.then_inc(s["conv_done"], 1)

        def flat(t3):
            return t3[:, :, :].rearrange("p h n -> p (h n)")

        def direction(m, d):
            r, i_, t_ = flat(gr[d]), flat(gi[d]), flat(gs[d])
            dve.wait_ge(s["gates_act"], 2 * m + d + 1)
            dve.wait_ge(s["conv_done"], m + 1)
            ch.step(V.tensor_scalar(gq[:, :], r, 1.0, None, ALU.add))
            ch.step(V.reciprocal(gq[:, :], gq[:, :]))
            ch.link(V.tensor_scalar(r, gq[:, :], 2.0, -1.0, ALU.mult, ALU.add))
            ch.link(V.tensor_tensor(i_, i_, xc[:, m % 2, :], ALU.mult))
            ch.step(V.scalar_tensor_tensor(out=t_, in0=t_, scalar=2.0, in1=gq[:, :], op0=ALU.mult, op1=ALU.mult))
            ch.step(V.tensor_tensor(t_, t_, i_, ALU.mult))
            h = hdir[d]
            for g, (c0, c1) in enumerate(((0, TA), (TA + GAP, TA + GAP + TB))):
                init = 0.0 if g == 0 else vecs[:, V_ST + d * 8 + m:V_ST + d * 8 + m + 1]
                if d == 0:
                    o_, a_, b_ = h[:, c0:c1], r[:, c0:c1], t_[:, c0:c1]
                elif c0 == 0:
                    o_, a_, b_ = h[:, c1 - 1::-1], r[:, c1 - 1::-1], t_[:, c1 - 1::-1]
                else:
                    o_, a_, b_ = h[:, c1 - 1:c0 - 1:-1], r[:, c1 - 1:c0 - 1:-1], t_[:, c1 - 1:c0 - 1:-1]
                last = V.tensor_tensor_scan(out=o_, data0=a_, data1=b_, initial=init, op0=ALU.mult, op1=ALU.add)
            last.then_inc(s["dir_done"], 1)
            dve.wait_ge(s["dir_done"], 2 * m + d + 1)
            e = TA - 1 if d == 0 else 0
            ins = V.tensor_copy(stfin[:, d, m:m + 1], h[:, e:e + 1])
            if m == KC - 1 and d == 1:
                ins.then_inc(s["st_ready"], 1)

        conv(0)
        for m in range(KC):
            if m + 1 < KC:
                conv(m + 1)
            for d in range(2):
                direction(m, d)
            for (c0, c1, o) in ((0, TA, 0), (TA, T, GAP)):
                last = V.tensor_tensor(hs[:, m, c0:c1], hdir[0][:, c0 + o:c1 + o], hdir[1][:, c0 + o:c1 + o], ALU.add)
            ch.step(last)
        for m in range(KC):
            dve.wait_ge(psum_free[m % 2], P_YR // 2 + m // 2 + 1)
            V.tensor_tensor(hs[:, m, :], hs[:, m, :], gy[:, m % 2, :], ALU.mult).then_inc(s["a_ready"], 1)
        dve.wait_ge(s["a_ready"], KC)
        los(S_A, KC, aLo, aHi, hs)

        with dve.Fori(0, KC // 2) as i:
            for b in range(2):
                m = i * 2 + b
                dve.wait_ge(psum_free[0], m + 11)
                dve.wait_ge(s["prod_done"], m * 4 + (P_MIX + 2))
                V.tensor_tensor(tm1.rearrange("p (h n) -> p h n", h=2), P[1][:, :, 0:HALF],
                                sga[:, b, :].rearrange("p (h n) -> p h n", h=2), ALU.mult).then_inc(psum_free[1], 1)
                dve.wait_ge(psum_free[2], m + 1)
                dve.wait_ge(s["prod_done"], m * 4 + (P_MIX + 4))
                V.tensor_tensor(tm2.rearrange("p (h n) -> p h n", h=2), P[3][:, :, 0:HALF],
                                sgb[:, b, :].rearrange("p (h n) -> p h n", h=2), ALU.mult).then_inc(psum_free[3], 1)
                dve.wait_ge(psum_free[1], m + 11)
                dve.wait_ge(psum_free[3], m + 1)
                V.tensor_tensor(hs[:, ds(m, 1), :].rearrange("p a n -> p (a n)"), tm1, tm2, ALU.add
                                ).then_inc(s["merged_ready"], 1)
                dve.wait_ge(s["merged_ready"], m + 1)
        los(S_MG, KC, hLo, hHi, hs)
        mods(1, B_G1, 16, 8)
        for m in range(KC):
            pr = m % 2
            dve.wait_ge(s["prod_done"], P_WO + m + 1)
            for (c0, c1, g) in ((0, TA, 0), (TA, HALF, 1), (HALF, T, 1)):
                h = c0 // HALF
                last = V.scalar_tensor_tensor(out=x[:, m, c0:c1], in0=P[pr][:, h, c0 - h * HALF:c1 - h * HALF],
                                              scalar=mod[:, 16 + m, g:g + 1], in1=x[:, m, c0:c1],
                                              op0=ALU.mult, op1=ALU.add)
            last.then_inc(psum_free[pr], 1)
        inv_rms(1)
        mods(2, B_MOD2, 24, 16)
        scale(scl2, 32, V_N2, s["mod_ready"])
        normed(1)
        los(S_H2, KC, hLo, hHi, hs)

        sel = Chain(dve, s["sel_c"], s["dve_held"])
        HC = NT * TOPK
        with dve.Fori(0, HEADS // 2) as hh:
            sel.enter(hh, 2 * 8)
            for par in range(2):
                h = hh * 2 + par
                hold(dve, s["S_ready"], hh * 4 + (2 * par + 2), s["dve_held"])
                with dve.Fori(0, NT) as t:
                    ch.enter(hh * (2 * NT) + (t + par * NT), 13)
                    sv = [S[:, par * 2 + p, ds(t * NKEY, NKEY)] for p in range(2)]

                    def each(fn):
                        ins = [fn(p) for p in range(2)]
                        ch.step(ins[-1])
                    V.tensor_copy(sw[:, 0, :], sv[0])
                    ch.step(V.tensor_copy(sw[:, 1, :], sv[1]))
                    each(lambda p: V.max(v8[:, p, 0:8], sw[:, p, :]))
                    each(lambda p: V.max_index(i8[:, p, 0:8], v8[:, p, 0:8], sw[:, p, :]))
                    each(lambda p: V.match_replace(sw[:, p, :], v8[:, p, 0:8], sw[:, p, :], BIG))
                    each(lambda p: V.max(v8[:, p, 8:16], sw[:, p, :]))
                    each(lambda p: V.max_index(i8[:, p, 8:16], v8[:, p, 8:16], sw[:, p, :]))
                    V.tensor_copy(i1f[:, 0:2, ds(t * TOPK, TOPK)], i8[:, 0:2, :])
                    ch.step(V.tensor_tensor(cand[:, :].rearrange("p (a b) -> p a b", a=TOPK),
                                            v8[:, 0, :].unsqueeze(2).broadcast_to([128, TOPK, TOPK]),
                                            v8[:, 1, :].unsqueeze(1).broadcast_to([128, TOPK, TOPK]), ALU.add))
                    ch.step(V.max(s16[:, 0:8], cand[:, :]))
                    ch.step(V.max_index(c16[:, 0:8], s16[:, 0:8], cand[:, :]))
                    ch.step(V.match_replace(cand[:, :], s16[:, 0:8], cand[:, :], BIG))
                    ch.step(V.max(s16[:, 8:16], cand[:, :]))
                    ch.step(V.max_index(c16[:, 8:16], s16[:, 8:16], cand[:, :]))
                    V.tensor_copy(SC[:, ds(t * SLOTS + h * TOPK, TOPK)], s16[:, :])
                    ch.step(V.tensor_copy(CI[:, ds(t * TOPK, TOPK)], c16[:, :]))
                V.tensor_scalar(ab[:, 0, :], CI[:, :], 4, None, ALU.logical_shift_right)
                sel.step(V.tensor_scalar(ab[:, 1, :], CI[:, :], 15, None, ALU.bitwise_and))
                sel.step(V.tensor_copy(abf[:, :, :], ab[:, :, :]))
                ohs = [oh[:, p, :].rearrange("p (a b) -> p a b", b=TOPK) for p in range(2)]
                for p in range(2):
                    sel.link(V.tensor_tensor(ohs[p], abf[:, p, :].unsqueeze(2).broadcast_to([128, HC, TOPK]),
                                             iota16[:, :].unsqueeze(1).broadcast_to([128, HC, TOPK]), ALU.is_equal))
                sel.wait()
                for p in range(2):
                    o4 = oh[:, p, :].rearrange("p (t a b) -> p t a b", t=NT, a=TOPK)
                    i4 = i1f[:, p, :].rearrange("p (t b) -> p t b", t=NT).unsqueeze(2).broadcast_to(
                        [128, NT, TOPK, TOPK])
                    ins = V.tensor_tensor(o4, o4, i4, ALU.mult)
                sel.step(ins)
                for p in range(2):
                    sel.link(V.tensor_reduce(esel[:, p, :], ohs[p], AX.X, ALU.add))
                sel.wait()
                sel.step(V.scalar_tensor_tensor(out=esel[:, 0, :], in0=esel[:, 0, :], scalar=float(NKEY),
                                                in1=esel[:, 1, :], op0=ALU.mult, op1=ALU.add))
                V.tensor_copy(E[:, :].rearrange("p (t s) -> p t s", t=NT)[:, :, ds(h * TOPK, TOPK)],
                              esel[:, 0, :].rearrange("p (t s) -> p t s", t=NT)).then_inc(s["head_done"], 1)
            assert sel.n == sel.per
        dve.wait_ge(s["head_done"], HEADS)
        ch.leave(HEADS * NT)
        sc3 = SC[:, :].rearrange("p (g k) -> p g k", k=TOPK)
        scm3 = SCm[:, :].rearrange("p (g k) -> p g k", k=TOPK)
        V.tensor_tensor(scm3, sc3, sc3[:, :, 0:1].broadcast_to([128, NT * HEADS, TOPK]), ALU.subtract
                        ).then_inc(s["scm_ready"], 1)
        V.memset(accB, 0.0).then_inc(s["e_ready"], 1)
        dve.wait_ge(s["exp_ready"], 1)
        ch.step(V.tensor_reduce(den[:, :], sc3, AX.X, ALU.add))
        ch.step(V.reciprocal(den[:, :], den[:, :]))
        ch.step(V.tensor_tensor(sc3, sc3, den[:, :].unsqueeze(2).broadcast_to([128, NT * HEADS, TOPK]), ALU.mult))
        dve.wait_ge(s["htok_ready"], NT)
        mods(3, B_G2, 40, 8)
        V.memset(accB, 0.0).then_inc(s["row_free"], UR)
        with dve.Fori(0, NT) as t:
            ht = htok[:, ds(t, 1), :].rearrange("p a n -> p (a n)")
            with dve.Fori(0, SLOTS // UR) as g:
                for j in range(UR):
                    dve.wait_ge(row_ld[j], t * (2 * SLOTS // UR * 16) + g * 16 + 16)
                    V.scalar_tensor_tensor(out=rows[:, j, :], in0=rows[:, j, :], scalar=1.0, in1=ht, op0=ALU.mult,
                                           op1=ALU.mult, accum_out=actv[:, ds(t * SLOTS + g * UR + j, 1)]
                                           ).then_inc(s["row_free"], 1)
            V.memset(accB, 0.0).then_inc(s["act_ready"], 1)
            dve.wait_ge(s["act_ready"], t + 1)
            V.tensor_copy(ht, accB)
            dve.wait_ge(s["gel_ready"], t + 1)
            V.tensor_tensor(wgt[:, ds(t * SLOTS, SLOTS)], wgt[:, ds(t * SLOTS, SLOTS)], SC[:, ds(t * SLOTS, SLOTS)],
                            ALU.mult).then_inc(s["wgt_ready"], 1)
            hold(dve, s["wgt_ready"], t + 1, s["dve_held"])
            with dve.Fori(0, SLOTS // UR) as g:
                for j in range(UR):
                    dve.wait_ge(row_ld[j], t * (2 * SLOTS // UR * 16) + g * 16 + (SLOTS // UR * 16 + 16))
                    dve.wait_ge(s["row_free"], t * (2 * SLOTS) + g * UR + (SLOTS + UR + j - 1))
                    a_ = ht if j % 2 == 0 else accB
                    V.scalar_tensor_tensor(out=a_, in0=rows[:, j, :], scalar=wgt[:, ds(t * SLOTS + g * UR + j, 1)],
                                           in1=a_, op0=ALU.mult, op1=ALU.add).then_inc(s["row_free"], 1)
            hold(dve, s["row_free"], t * (2 * SLOTS) + (2 * SLOTS + UR), s["dve_held"])
            V.tensor_tensor(ht, ht, accB, ALU.add).then_inc(s["acc_ready"], 1)
            hold(dve, s["acc_ready"], t + 1, s["dve_held"])
        for t in range(NT):
            dve.wait_ge(s["accT_done"], t + 1)
            for k in range(KC):
                last = V.scalar_tensor_tensor(
                    out=x[:, k, t * 128:(t + 1) * 128],
                    in0=P[(t % 2) * 2][:, k // 4, (k % 4) * 128:(k % 4 + 1) * 128],
                    scalar=mod[:, 40 + k, min(t, 1):min(t, 1) + 1], in1=x[:, k, t * 128:(t + 1) * 128],
                    op0=ALU.mult, op1=ALU.add)
            last.then_inc(s["x3_ready"], 1)
        dve.wait_ge(s["x3_ready"], NT)
        inv_rms(2)
        with dve.Fori(0, KC) as k:
            V.scalar_tensor_tensor(out=hs[:, ds(k, 1), :].rearrange("p a n -> p (a n)"),
                                   in0=x[:, ds(k, 1), :].rearrange("p a n -> p (a n)"),
                                   scalar=vecs[:, ds(k + V_FG, 1)], in1=rstd[:, :],
                                   op0=ALU.mult, op1=ALU.mult).then_inc(s["y_ready"], 1)

    block.__exit__(None, None, None)


def layout(inputs):
    import numpy as np
    a = {k: np.asarray(v) for k, v in inputs.items()}
    c_ = np.ascontiguousarray

    def feat(v, n):
        return v.reshape(n, 128).T

    def blocks(w, order=None):
        K, M = w.shape
        b = w.reshape(K // 128, 128, M // 128, 128).transpose(2, 1, 0, 3).reshape(M // 128, 128, K)
        return b

    x_all = np.concatenate([a["x_prompt"][0], a["x_sample"][0]], 0)
    xT = x_all.T.reshape(KC, 128, T).transpose(1, 0, 2)
    nq, gridw = D // 4, 64
    omega = (1.0 / (np.float32(10000.0) ** (np.arange(nq, dtype=np.float32) / np.float32(nq)))).astype(np.float32)
    r = np.repeat(np.arange(TB // gridw, dtype=np.float32), gridw)
    cc = np.tile(np.arange(gridw, dtype=np.float32), TB // gridw)
    er, ec = r[:, None] * omega[None], cc[:, None] * omega[None]
    pos = np.concatenate([np.sin(er), np.cos(er), np.sin(ec), np.cos(ec)], -1).astype(np.float32)
    posT = pos.T.reshape(KC, 128, TB).transpose(1, 0, 2)
    cT = np.stack([feat(a["c_ctx"], KC), feat(a["c"][0], KC)], -1).reshape(128, 2 * KC)
    vecs = np.concatenate([feat(a["norm1_g"][0], 8), feat(a["norm2_g"][0], 8), feat(a["b_mod"][0], 48),
                           feat(a["conv_w"][0].reshape(-1), 32), feat(a["conv_b"][0], 8),
                           feat(a["rg_ba"][0].reshape(-1), 16), feat(a["rg_bx"][0].reshape(-1), 16),
                           feat(a["rg_lambda"][0].reshape(-1), 16), feat(a["pool_b"][0], 4),
                           feat(a["pool_scale"][0], 4), feat(a["final_g"], 8),
                           feat(a["state_rglru"][0, 0].reshape(-1), 16)], 1)
    iota = np.broadcast_to(np.arange(16, dtype=np.float32), (128, 16))
    t_all = []
    for L in (TA, TB):
        t = np.arange(L)
        t_all.append([np.minimum(t + w // 2, L) - np.maximum(t - w // 2, 0) for w in (2, 4, 8, 16)])
    cnt = np.concatenate([np.array(t_all[0]), np.array(t_all[1])], 1)
    invc = np.broadcast_to((1.0 / cnt).astype(np.float32)[None], (128, 4, T))
    gw = np.zeros((128, 2, 2, 8, 128), np.float32)
    for kind, name in enumerate(("rg_wa", "rg_wx")):
        w = a[name][0].reshape(2, 8, 2, 64, 64)
        for hh in range(2):
            gw[hh * 64:(hh + 1) * 64, :, kind, :, hh * 64:(hh + 1) * 64] = w[:, :, hh].transpose(2, 0, 1, 3)
    gw = gw.reshape(128, 32, 128)
    pw = a["pool_w"][0].transpose(1, 0, 2)
    keysT = a["peer_keys"][0].reshape(16, NKEY, 128).transpose(2, 0, 1)
    win, wmod = blocks(a["w_in"][0]), blocks(a["w_mod"][0])
    up_r, up_p = blocks(a["w_up_rnn"][0]), blocks(a["w_up_pool"][0])
    up_p = np.concatenate([up_p, np.zeros_like(up_p)], -1)
    mix = np.stack([win[20:28], up_r, win[28:36], up_p], 1).reshape(32, 128, D)
    w_all = np.concatenate([wmod[0:16], win[16:20], win[0:8], win[8:16], mix, wmod[16:24], blocks(a["w_o"][0]),
                            wmod[24:40], blocks(a["peer_wq"][0]), wmod[40:48]], 0)
    out = dict(xT=xT, posT=posT, cT=cT, vecs=vecs, iota=iota, invc=invc, gw=gw, pw=pw, keysT=keysT, wblk=w_all,
               u_tab=a["peer_u"][0], v_tab=a["peer_v"][0], ident=np.eye(128, dtype=np.float32))
    return {k: c_(v, dtype=np.float32) for k, v in out.items()}


def kernel(**inputs):
    import numpy as np
    import concourse.bacc as bacc
    from concourse.bass_utils import run_bass_kernel_spmd

    nc = bacc.Bacc("TRN2", target_bir_lowering=False, num_devices=1)
    arrays = layout(inputs)
    f32 = mybir.dt.float32
    args = [nc.dram_tensor("in_" + n, a.shape, f32, kind="ExternalInput").ap() for n, a in arrays.items()]
    args.append(nc.dram_tensor("yT", (128, KC, T), f32, kind="ExternalOutput").ap())
    args.append(nc.dram_tensor("st", (128, 2, KC), f32, kind="ExternalOutput").ap())
    build(nc, *args)
    got = run_bass_kernel_spmd(nc, [{"in_" + n: a for n, a in arrays.items()}], core_ids=[0]).results[0]
    y = np.asarray(got["yT"]).transpose(2, 1, 0).reshape(T, D)
    st = np.asarray(got["st"]).transpose(1, 2, 0).reshape(1, 1, 2, D)
    return (np.ascontiguousarray(y[None, :TA]), np.ascontiguousarray(y[None, TA:]), np.ascontiguousarray(st))
```
